# Optimizing a Trainium2 kernel written in Bass

```python
import math
import jax, jax.numpy as jnp
from jax import lax
import numpy as np

D_MODEL = 1024
BATCH = 1
SEQ = 256
DEPTH = 2

CTX_LEN = 256
GRID_W = 64
EPS = 1e-6

MLSTM_HEADS = 4
MLSTM_HEAD_DIM = D_MODEL // 8
MLSTM_WIDTH = MLSTM_HEADS * MLSTM_HEAD_DIM
MLSTM_CHUNK = 128
FORGET_BIAS = 4.0
SGU_GROUPS = 4
SGU_WIDTH = D_MODEL // 4
SGU_CHUNK = 128
CONV_WIDTH = D_MODEL // 4
CONV_K = 31

MIX_WIDTH = MLSTM_WIDTH + SGU_WIDTH + CONV_WIDTH
FFN_HIDDEN = int(math.ceil(8 * D_MODEL / 3 / 256)) * 256

Q_OFF = 0
K_OFF = MLSTM_WIDTH
V_OFF = 2 * MLSTM_WIDTH
O_OFF = 3 * MLSTM_WIDTH
GATE_OFF = 4 * MLSTM_WIDTH
SGU_OFF = GATE_OFF + 4 * MLSTM_HEADS
CONV_OFF = SGU_OFF + 2 * SGU_WIDTH
IN_COLS = CONV_OFF + 2 * CONV_WIDTH


def rmsnorm(t, g):
    t32 = t.astype(jnp.float32)
    y = t32 * lax.rsqrt(jnp.mean(t32 * t32, axis=-1, keepdims=True) + EPS)
    return (y * g).astype(t.dtype)

def layernorm(t, g, b):
    t32 = t.astype(jnp.float32)
    mu = jnp.mean(t32, axis=-1, keepdims=True)
    d = t32 - mu
    var = jnp.mean(d * d, axis=-1, keepdims=True)
    return (d * lax.rsqrt(var + EPS) * g + b).astype(t.dtype)

def swiglu(h, w_gu, w_down):
    gate, up = jnp.split(h @ w_gu, 2, axis=-1)
    return (jax.nn.silu(gate) * up) @ w_down

def mlstm_inputs(p):
    B, L, _ = p.shape
    def heads(t):
        return t.reshape(B, L, MLSTM_HEADS, MLSTM_HEAD_DIM).transpose(0, 2, 1, 3).astype(jnp.float32)
    q = heads(p[..., Q_OFF:K_OFF])
    k = heads(p[..., K_OFF:V_OFF]) * (MLSTM_HEAD_DIM ** -0.5)
    v = heads(p[..., V_OFF:O_OFF])
    g = p[..., GATE_OFF:SGU_OFF].astype(jnp.float32).reshape(B, L, 4, MLSTM_HEADS).transpose(2, 0, 3, 1)
    gates = (g[0], jax.nn.log_sigmoid(g[1]), g[2], jax.nn.log_sigmoid(g[3]))
    return q, k, v, gates

def zero_state(batch):
    return (jnp.zeros((batch, MLSTM_HEADS, MLSTM_HEAD_DIM, MLSTM_HEAD_DIM), jnp.float32),
            jnp.zeros((batch, MLSTM_HEADS, MLSTM_HEAD_DIM), jnp.float32),
            jnp.zeros((batch, MLSTM_HEADS), jnp.float32))

def mlstm_scan(q, k, v, logi, logf, state, with_output):
    B, H, L, d = q.shape
    nc = L // MLSTM_CHUNK
    def to_chunks(t):
        t = t.reshape((B, H, nc, MLSTM_CHUNK) + t.shape[3:])
        return jnp.moveaxis(t, 2, 0)
    xs = tuple(to_chunks(t) for t in (q, k, v, logi, logf))
    order = jnp.tril(jnp.ones((MLSTM_CHUNK, MLSTM_CHUNK), bool))

    def step(carry, inp):
        C, n, m = carry
        qc, kc, vc, ic, fc = inp
        b = jnp.cumsum(fc, axis=-1)
        b_last = b[..., -1]
        w_log = b_last[..., None] - b + ic
        m_new = jnp.maximum(b_last + m, jnp.max(w_log, axis=-1))
        decay = jnp.exp(b_last + m - m_new)
        ks = kc * jnp.exp(w_log - m_new[..., None])[..., None]
        C_new = decay[..., None, None] * C + jnp.einsum('bhsk,bhsv->bhkv', ks, vc)
        n_new = decay[..., None] * n + jnp.sum(ks, axis=2)
        if not with_output:
            return (C_new, n_new, m_new), None
        a = b + m[..., None]
        Dlog = b[..., :, None] - b[..., None, :] + ic[..., None, :]
        Dlog = jnp.where(order, Dlog, -jnp.inf)
        m_t = jnp.maximum(a, jnp.max(Dlog, axis=-1))
        w_inter = jnp.exp(a - m_t)
        s = jnp.einsum('bhtk,bhsk->bhts', qc, kc) * jnp.exp(Dlog - m_t[..., None])
        num = w_inter[..., None] * jnp.einsum('bhtk,bhkv->bhtv', qc, C) + jnp.einsum('bhts,bhsv->bhtv', s, vc)
        den = w_inter * jnp.einsum('bhtk,bhk->bht', qc, n) + jnp.sum(s, axis=-1)
        h = num / jnp.maximum(jnp.abs(den), jnp.exp(-m_t))[..., None]
        return (C_new, n_new, m_new), h

    state, hs = lax.scan(step, state, xs)
    if not with_output:
        return None, state
    h = jnp.moveaxis(hs, 0, 2).reshape(B, H, L, d)
    return h, state

def _flip(t):
    return jnp.flip(t, axis=2)

def mlstm_bidir(q, k, v, gates, init_f, init_b, with_output):
    logi_f, logf_f, logi_b, logf_b = gates
    h_f, st_f = mlstm_scan(q, k, v, logi_f, logf_f, init_f, with_output)
    h_b, st_b = mlstm_scan(_flip(q), _flip(k), _flip(v), _flip(logi_b), _flip(logf_b), init_b, with_output)
    h = h_f + _flip(h_b) if with_output else None
    return h, st_f, st_b

def mlstm_post(h, o_pre, g):
    B, H, L, d = h.shape
    h = h * lax.rsqrt(jnp.mean(h * h, axis=-1, keepdims=True) + EPS)
    h = h.transpose(0, 2, 1, 3).reshape(B, L, H * d) * g
    return (h * jax.nn.sigmoid(o_pre.astype(jnp.float32))).astype(o_pre.dtype)

def chunk_sgu(z, ln_g, ln_b, w_s, b_s):
    z = jax.nn.gelu(z)
    u, v = jnp.split(z, 2, axis=-1)
    v = layernorm(v, ln_g, ln_b)
    B, L, C = v.shape
    vg = v.reshape(B, L // SGU_CHUNK, SGU_CHUNK, SGU_GROUPS, C // SGU_GROUPS)
    mixed = jnp.einsum('gpq,bnqgc->bnpgc', w_s, vg) + b_s.T[:, :, None]
    return u * mixed.reshape(B, L, C)

def dwconv1d(y, w, b):
    kw, ch = w.shape
    out = lax.conv_general_dilated(y, w.reshape(kw, 1, ch).astype(y.dtype), window_strides=(1,),
                                   padding=[(kw // 2, kw // 2)], dimension_numbers=('NWC', 'WIO', 'NWC'),
                                   feature_group_count=ch)
    return out + b

def axial_dwconv(y, w, b):
    B, L, C = y.shape
    rows = L // GRID_W
    half = C // 2
    yr = dwconv1d(y[..., :half].reshape(B * rows, GRID_W, half), w[:, :half], b[:half]).reshape(B, L, half)
    yc = y[..., half:].reshape(B, rows, GRID_W, half).transpose(0, 2, 1, 3).reshape(B * GRID_W, rows, half)
    yc = dwconv1d(yc, w[:, half:], b[half:]).reshape(B, GRID_W, rows, half).transpose(0, 2, 1, 3).reshape(B, L, half)
    return jnp.concatenate([yr, yc], axis=-1)

def conformer_conv(z, w_dw, b_dw, ln_g, ln_b, grid):
    a, g = jnp.split(z, 2, axis=-1)
    y = a * jax.nn.sigmoid(g)
    y = axial_dwconv(y, w_dw, b_dw) if grid else dwconv1d(y, w_dw, b_dw)
    return jax.nn.silu(layernorm(y, ln_g, ln_b))

def mix_groups(p, h_mlstm, mlstm_g, sgu_ln_g, sgu_ln_b, sgu_w, sgu_b, conv_w, conv_b, conv_ln_g, conv_ln_b, grid):
    y_a = mlstm_post(h_mlstm, p[..., O_OFF:GATE_OFF], mlstm_g)
    y_b = chunk_sgu(p[..., SGU_OFF:CONV_OFF], sgu_ln_g, sgu_ln_b, sgu_w, sgu_b)
    y_c = conformer_conv(p[..., CONV_OFF:IN_COLS], conv_w, conv_b, conv_ln_g, conv_ln_b, grid)
    return jnp.concatenate([y_a, y_b, y_c], axis=-1)

def first_inputs(seed: int = 0) -> dict:
    key = jax.random.key(seed)
    ks = jax.random.split(key, 24)
    def nrm(k, shape, scale):
        return jax.random.normal(k, shape, jnp.float32) * scale
    fb = np.zeros((IN_COLS,), np.float32)
    fb[GATE_OFF + MLSTM_HEADS:GATE_OFF + 2 * MLSTM_HEADS] = FORGET_BIAS
    fb[GATE_OFF + 3 * MLSTM_HEADS:GATE_OFF + 4 * MLSTM_HEADS] = FORGET_BIAS
    return {
        'x': nrm(ks[0], (BATCH, SEQ, D_MODEL), 1.0),
        'c': nrm(ks[1], (BATCH, D_MODEL), 1.0),
        'ctx': nrm(ks[2], (BATCH, CTX_LEN, D_MODEL), 1.0),
        'c_ctx': nrm(ks[3], (D_MODEL,), 1.0),
        'w_mod': nrm(ks[4], (DEPTH, D_MODEL, 6 * D_MODEL), 0.5 * D_MODEL ** -0.5),
        'b_mod': nrm(ks[5], (DEPTH, 6 * D_MODEL), 0.02),
        'norm1_g': 1.0 + nrm(ks[6], (DEPTH, D_MODEL), 0.02),
        'w_in': nrm(ks[7], (DEPTH, D_MODEL, IN_COLS), D_MODEL ** -0.5),
        'b_in': nrm(ks[8], (DEPTH, IN_COLS), 0.02) + jnp.asarray(fb),
        'mlstm_g': 1.0 + nrm(ks[9], (DEPTH, MLSTM_WIDTH), 0.02),
        'sgu_ln_g': 1.0 + nrm(ks[10], (DEPTH, SGU_WIDTH), 0.02),
        'sgu_ln_b': nrm(ks[11], (DEPTH, SGU_WIDTH), 0.02),
        'sgu_w': nrm(ks[12], (DEPTH, SGU_GROUPS, SGU_CHUNK, SGU_CHUNK), SGU_CHUNK ** -0.5),
        'sgu_b': nrm(ks[13], (DEPTH, SGU_GROUPS, SGU_CHUNK), 0.02),
        'conv_w': nrm(ks[14], (DEPTH, CONV_K, CONV_WIDTH), CONV_K ** -0.5),
        'conv_b': nrm(ks[15], (DEPTH, CONV_WIDTH), 0.02),
        'conv_ln_g': 1.0 + nrm(ks[16], (DEPTH, CONV_WIDTH), 0.02),
        'conv_ln_b': nrm(ks[17], (DEPTH, CONV_WIDTH), 0.02),
        'w_out': nrm(ks[18], (DEPTH, MIX_WIDTH, D_MODEL), MIX_WIDTH ** -0.5),
        'norm2_g': 1.0 + nrm(ks[19], (DEPTH, D_MODEL), 0.02),
        'w_gu': nrm(ks[20], (DEPTH, D_MODEL, 2 * FFN_HIDDEN), D_MODEL ** -0.5),
        'w_down': nrm(ks[21], (DEPTH, FFN_HIDDEN, D_MODEL), FFN_HIDDEN ** -0.5),
        'final_g': 1.0 + nrm(ks[22], (D_MODEL,), 0.02),
    }

def first_block(x, c, ctx, c_ctx, w_mod, b_mod, norm1_g, w_in, b_in, mlstm_g, sgu_ln_g, sgu_ln_b, sgu_w, sgu_b,
              conv_w, conv_b, conv_ln_g, conv_ln_b, w_out, norm2_g, w_gu, w_down, final_g):
    batch = x.shape[0]
    c_act = jax.nn.silu(c)
    cc_act = jax.nn.silu(c_ctx)
    xc = ctx
    for l in range(DEPTH):
        last = l == DEPTH - 1
        mod = (c_act @ w_mod[l] + b_mod[l])[:, None, :]
        modc = cc_act @ w_mod[l] + b_mod[l]
        sh1, sc1, g1, sh2, sc2, g2 = jnp.split(mod, 6, axis=-1)
        shc1, scc1, gc1, shc2, scc2, gc2 = jnp.split(modc, 6, axis=-1)

        px = (rmsnorm(x, norm1_g[l]) * (1.0 + sc1) + sh1) @ w_in[l] + b_in[l]
        pc = (rmsnorm(xc, norm1_g[l]) * (1.0 + scc1) + shc1) @ w_in[l] + b_in[l]
        qx, kx, vx, gtx = mlstm_inputs(px)
        qc, kc, vc, gtc = mlstm_inputs(pc)
        zs = zero_state(batch)
        h_c, st_f, st_b = mlstm_bidir(qc, kc, vc, gtc, zs, zs, not last)
        h_x, _, _ = mlstm_bidir(qx, kx, vx, gtx, st_f, st_b, True)

        y_x = mix_groups(px, h_x, mlstm_g[l], sgu_ln_g[l], sgu_ln_b[l], sgu_w[l], sgu_b[l],
                         conv_w[l], conv_b[l], conv_ln_g[l], conv_ln_b[l], True)
        x = x + g1 * (y_x @ w_out[l])
        x = x + g2 * swiglu(rmsnorm(x, norm2_g[l]) * (1.0 + sc2) + sh2, w_gu[l], w_down[l])

        if not last:
            y_c = mix_groups(pc, h_c, mlstm_g[l], sgu_ln_g[l], sgu_ln_b[l], sgu_w[l], sgu_b[l],
                             conv_w[l], conv_b[l], conv_ln_g[l], conv_ln_b[l], False)
            xc = xc + gc1 * (y_c @ w_out[l])
            xc = xc + gc2 * swiglu(rmsnorm(xc, norm2_g[l]) * (1.0 + scc2) + shc2, w_gu[l], w_down[l])
    return rmsnorm(x, final_g)


HEAD_DIM = 64
N_HEADS = D_MODEL // HEAD_DIM
HEADS_A = N_HEADS // 2
HEADS_B = N_HEADS - HEADS_A
GQA_GROUP = 4
KV_A = HEADS_A // GQA_GROUP
KV_B = HEADS_B // GQA_GROUP
WINDOW = 128
Q_BLOCK = 128
HEADS_C = D_MODEL // (2 * HEAD_DIM)
FFN_HIDDEN_2 = ((8 * D_MODEL // 3 + 255) // 256) * 256
ROPE_THETA = 10000.0
NEG_INF = -1e30
N_EVEN = (DEPTH + 1) // 2
N_ODD = DEPTH // 2
EVEN_IN = (HEADS_A + 2 * KV_A + HEADS_B + 2 * KV_B) * HEAD_DIM
EVEN_OUT = (HEADS_A + HEADS_B) * HEAD_DIM
ODD_IN = 3 * 2 * HEADS_C * HEAD_DIM
ODD_OUT = HEADS_C * 2 * HEAD_DIM


def _rms(x, w):
    xf = x.astype(jnp.float32)
    y = xf * lax.rsqrt(jnp.mean(xf * xf, axis=-1, keepdims=True) + EPS)
    return (y * w.astype(jnp.float32)).astype(x.dtype)

def _axial_tables(rows):
    row = jnp.repeat(jnp.arange(rows, dtype=jnp.float32), GRID_W)
    col = jnp.tile(jnp.arange(GRID_W, dtype=jnp.float32), rows)
    n_freq = HEAD_DIM // 4
    inv = ROPE_THETA ** (-jnp.arange(n_freq, dtype=jnp.float32) / n_freq)
    ang = jnp.concatenate([row[:, None] * inv, col[:, None] * inv], axis=-1)
    return jnp.cos(ang), jnp.sin(ang)

def _rope(x, cos, sin):
    n = x.shape[1]
    bshape = (1, n) + (1,) * (x.ndim - 3) + (HEAD_DIM // 2,)
    c = cos.reshape(bshape).astype(x.dtype)
    s = sin.reshape(bshape).astype(x.dtype)
    xp = x.reshape(*x.shape[:-1], HEAD_DIM // 2, 2)
    x0, x1 = xp[..., 0], xp[..., 1]
    return jnp.stack([x0 * c - x1 * s, x0 * s + x1 * c], axis=-1).reshape(x.shape)

def _softmax(s, sink):
    if sink is None:
        return jax.nn.softmax(s, axis=-1)
    m = jnp.maximum(jnp.max(s, axis=-1, keepdims=True), sink)
    p = jnp.exp(s - m)
    return p / (jnp.sum(p, axis=-1, keepdims=True) + jnp.exp(sink - m))

def _to_blocks(q):
    b, n = q.shape[:2]
    return jnp.moveaxis(q.reshape(b, n // Q_BLOCK, Q_BLOCK, *q.shape[2:]), 1, 0)

def _from_blocks(o):
    o = jnp.moveaxis(o, 0, 1)
    return o.reshape(o.shape[0], o.shape[1] * o.shape[2], -1)

def _window_attend(q, k_lat, v_lat, k_ctx, v_ctx, sink):
    n = q.shape[1]
    n_ctx = k_ctx.shape[1]
    span = Q_BLOCK + 2 * WINDOW
    pad = ((0, 0), (WINDOW, WINDOW), (0, 0), (0, 0))
    k_pad = jnp.pad(k_lat, pad)
    v_pad = jnp.pad(v_lat, pad)
    scale = HEAD_DIM ** -0.5
    sink_b = sink.astype(jnp.float32)[None, :, :, None, None]

    def one_block(args):
        qb, i = args
        start = i * Q_BLOCK
        kw = lax.dynamic_slice_in_dim(k_pad, start, span, axis=1)
        vw = lax.dynamic_slice_in_dim(v_pad, start, span, axis=1)
        qpos = start + jnp.arange(Q_BLOCK)
        kpos = start - WINDOW + jnp.arange(span)
        ok = (jnp.abs(qpos[:, None] - kpos[None, :]) <= WINDOW) & (kpos[None, :] >= 0) & (kpos[None, :] < n)
        s_c = jnp.einsum('bqhgd,bkhd->bhgqk', qb, k_ctx).astype(jnp.float32) * scale
        s_w = jnp.einsum('bqhgd,bkhd->bhgqk', qb, kw).astype(jnp.float32) * scale
        s_w = jnp.where(ok, s_w, NEG_INF)
        p = _softmax(jnp.concatenate([s_c, s_w], axis=-1), sink_b).astype(v_lat.dtype)
        return (jnp.einsum('bhgqk,bkhd->bqhgd', p[..., :n_ctx], v_ctx)
                + jnp.einsum('bhgqk,bkhd->bqhgd', p[..., n_ctx:], vw))

    out = lax.map(one_block, (_to_blocks(q), jnp.arange(n // Q_BLOCK)))
    return _from_blocks(out)

def _dense_attend(q, k, v, sink):
    scale = HEAD_DIM ** -0.5
    sink_b = None if sink is None else sink.astype(jnp.float32)[None, :, :, None, None]

    def one_block(qb):
        s = jnp.einsum('bqhgd,bkhd->bhgqk', qb, k).astype(jnp.float32) * scale
        p = _softmax(s, sink_b).astype(v.dtype)
        return jnp.einsum('bhgqk,bkhd->bqhgd', p, v)

    return _from_blocks(lax.map(one_block, _to_blocks(q)))

def _diff_attend(q, k, v, lam):
    scale = HEAD_DIM ** -0.5

    def one_block(qb):
        s = jnp.einsum('bqhad,bkhad->bhaqk', qb, k).astype(jnp.float32) * scale
        p = jax.nn.softmax(s, axis=-1)
        a = (p[:, :, 0] - lam * p[:, :, 1]).astype(v.dtype)
        return jnp.einsum('bhqk,bkhe->bqhe', a, v)

    out = lax.map(one_block, _to_blocks(q))
    out = jnp.moveaxis(out, 0, 1)
    return out.reshape(out.shape[0], out.shape[1] * out.shape[2], *out.shape[3:])

def _even_mixer(hx, hc, w_in, w_out, qn_a, kn_a, qn_b, kn_b, sink_a, cos, sin, with_ctx):
    d = HEAD_DIM
    cuts = [int(v) for v in np.cumsum([HEADS_A * d, KV_A * d, KV_A * d, HEADS_B * d, KV_B * d])]

    def heads(p, use_rope):
        b, n = p.shape[:2]
        qa, ka, va, qb, kb, vb = jnp.split(p, cuts, axis=-1)
        qa = _rms(qa.reshape(b, n, HEADS_A, d), qn_a)
        ka = _rms(ka.reshape(b, n, KV_A, d), kn_a)
        qb = _rms(qb.reshape(b, n, HEADS_B, d), qn_b)
        kb = _rms(kb.reshape(b, n, KV_B, d), kn_b)
        if use_rope:
            qa, ka, qb, kb = _rope(qa, cos, sin), _rope(ka, cos, sin), _rope(qb, cos, sin), _rope(kb, cos, sin)
        return (qa.reshape(b, n, KV_A, GQA_GROUP, d), ka, va.reshape(b, n, KV_A, d),
                qb.reshape(b, n, KV_B, GQA_GROUP, d), kb, vb.reshape(b, n, KV_B, d))

    qa_x, ka_x, va_x, qb_x, kb_x, vb_x = heads(hx @ w_in, True)
    qa_c, ka_c, va_c, qb_c, kb_c, vb_c = heads(hc @ w_in, False)
    sink = sink_a.reshape(KV_A, GQA_GROUP)
    oa_x = _window_attend(qa_x, ka_x, va_x, ka_c, va_c, sink)
    ob_x = _dense_attend(qb_x, jnp.concatenate([kb_c, kb_x], axis=1),
                         jnp.concatenate([vb_c, vb_x], axis=1), None)
    out_x = jnp.concatenate([oa_x, ob_x], axis=-1) @ w_out
    out_c = None
    if with_ctx:
        oa_c = _dense_attend(qa_c, ka_c, va_c, sink)
        ob_c = _dense_attend(qb_c, kb_c, vb_c, None)
        out_c = jnp.concatenate([oa_c, ob_c], axis=-1) @ w_out
    return out_x, out_c

def _odd_mixer(hx, hc, w_in, w_out, qn, kn, lq1, lk1, lq2, lk2, subln_w, lam_init, cos, sin, with_ctx):
    d = HEAD_DIM
    qs = 2 * HEADS_C * d

    def heads(p, use_rope):
        b, n = p.shape[:2]
        q, k, v = jnp.split(p, [qs, 2 * qs], axis=-1)
        q = _rms(q.reshape(b, n, HEADS_C, 2, d), qn)
        k = _rms(k.reshape(b, n, HEADS_C, 2, d), kn)
        if use_rope:
            q, k = _rope(q, cos, sin), _rope(k, cos, sin)
        return q, k, v.reshape(b, n, HEADS_C, 2 * d)

    q_x, k_x, v_x = heads(hx @ w_in, True)
    q_c, k_c, v_c = heads(hc @ w_in, False)
    f32 = jnp.float32
    lam = (jnp.exp(jnp.sum(lq1.astype(f32) * lk1.astype(f32)))
           - jnp.exp(jnp.sum(lq2.astype(f32) * lk2.astype(f32))) + lam_init)

    def finish(o):
        o = _rms(o, subln_w) * (1.0 - lam_init)
        return o.reshape(o.shape[0], o.shape[1], -1) @ w_out

    o_x = _diff_attend(q_x, jnp.concatenate([k_c, k_x], axis=1), jnp.concatenate([v_c, v_x], axis=1), lam)
    out_x = finish(o_x)
    out_c = None
    if with_ctx:
        out_c = finish(_diff_attend(q_c, k_c, v_c, lam))
    return out_x, out_c

def _swiglu(h, w_in, w_out):
    gate, up = jnp.split(h @ w_in, 2, axis=-1)
    return (jax.nn.silu(gate) * up) @ w_out

def second_inputs(seed: int = 0) -> dict:
    key = jax.random.key(seed)
    ks = jax.random.split(key, 26)
    f32 = jnp.float32

    def nrm(k, shape, s):
        return jax.random.normal(k, shape, f32) * s

    def gain(k, shape):
        return 1.0 + 0.02 * jax.random.normal(k, shape, f32)

    D, F, d = D_MODEL, FFN_HIDDEN_2, HEAD_DIM
    return {
        "x": nrm(ks[0], (BATCH, SEQ, D), 1.0),
        "c": nrm(ks[1], (BATCH, D), 1.0),
        "ctx": nrm(ks[2], (BATCH, CTX_LEN, D), 1.0),
        "c_ctx": nrm(ks[3], (D,), 1.0),
        "mod_w": nrm(ks[4], (DEPTH, D, 6 * D), 0.5 * D ** -0.5),
        "mod_b": nrm(ks[5], (DEPTH, 6 * D), 0.02),
        "norm_mix_w": gain(ks[6], (DEPTH, D)),
        "norm_ffn_w": gain(ks[7], (DEPTH, D)),
        "ev_w_in": nrm(ks[8], (N_EVEN, D, EVEN_IN), D ** -0.5),
        "ev_w_out": nrm(ks[9], (N_EVEN, EVEN_OUT, D), EVEN_OUT ** -0.5),
        "ev_qn_a": gain(ks[10], (N_EVEN, d)),
        "ev_kn_a": gain(ks[11], (N_EVEN, d)),
        "ev_qn_b": gain(ks[12], (N_EVEN, d)),
        "ev_kn_b": gain(ks[13], (N_EVEN, d)),
        "ev_sink_a": nrm(ks[14], (N_EVEN, HEADS_A), 0.5),
        "od_w_in": nrm(ks[15], (N_ODD, D, ODD_IN), D ** -0.5),
        "od_w_out": nrm(ks[16], (N_ODD, ODD_OUT, D), ODD_OUT ** -0.5),
        "od_qn": gain(ks[17], (N_ODD, d)),
        "od_kn": gain(ks[18], (N_ODD, d)),
        "od_lq1": nrm(ks[19], (N_ODD, d), 0.1),
        "od_lk1": nrm(ks[20], (N_ODD, d), 0.1),
        "od_lq2": nrm(ks[21], (N_ODD, d), 0.1),
        "od_lk2": nrm(ks[22], (N_ODD, d), 0.1),
        "od_subln": gain(ks[23], (N_ODD, 2 * d)),
        "ffn_w_in": nrm(ks[24], (DEPTH, D, 2 * F), D ** -0.5),
        "ffn_w_out": nrm(ks[25], (DEPTH, F, D), F ** -0.5),
    }

def second_block(x, c, ctx, c_ctx, mod_w, mod_b, norm_mix_w, norm_ffn_w,
              ev_w_in, ev_w_out, ev_qn_a, ev_kn_a, ev_qn_b, ev_kn_b, ev_sink_a,
              od_w_in, od_w_out, od_qn, od_kn, od_lq1, od_lk1, od_lq2, od_lk2, od_subln,
              ffn_w_in, ffn_w_out):
    n_lat = x.shape[1]
    ROWS = n_lat // GRID_W
    cos, sin = _axial_tables(ROWS)
    s_c = jax.nn.silu(c)
    s_cc = jax.nn.silu(c_ctx)[None, :]
    for l in range(DEPTH):
        last = l == DEPTH - 1
        i = l // 2
        mx = (s_c @ mod_w[l] + mod_b[l])[:, None, :]
        mc = (s_cc @ mod_w[l] + mod_b[l])[:, None, :]
        shx1, scx1, gx1, shx2, scx2, gx2 = jnp.split(mx, 6, axis=-1)
        shc1, scc1, gc1, shc2, scc2, gc2 = jnp.split(mc, 6, axis=-1)
        hx = _rms(x, norm_mix_w[l]) * (1.0 + scx1) + shx1
        hc = _rms(ctx, norm_mix_w[l]) * (1.0 + scc1) + shc1
        if l % 2 == 0:
            ax, ac = _even_mixer(hx, hc, ev_w_in[i], ev_w_out[i], ev_qn_a[i], ev_kn_a[i],
                                 ev_qn_b[i], ev_kn_b[i], ev_sink_a[i], cos, sin, not last)
        else:
            lam_init = 0.8 - 0.6 * math.exp(-0.3 * l)
            ax, ac = _odd_mixer(hx, hc, od_w_in[i], od_w_out[i], od_qn[i], od_kn[i],
                                od_lq1[i], od_lk1[i], od_lq2[i], od_lk2[i], od_subln[i],
                                lam_init, cos, sin, not last)
        x = x + gx1 * ax
        x = x + gx2 * _swiglu(_rms(x, norm_ffn_w[l]) * (1.0 + scx2) + shx2, ffn_w_in[l], ffn_w_out[l])
        if not last:
            ctx = ctx + gc1 * ac
            ctx = ctx + gc2 * _swiglu(_rms(ctx, norm_ffn_w[l]) * (1.0 + scc2) + shc2, ffn_w_in[l], ffn_w_out[l])
    return x


def setup_inputs(seed=0):
    out = dict(first_inputs(seed))
    for name, value in second_inputs(seed + 1).items():
        if name != "x":
            out[name + "_2"] = value
    return out


def reference(
    x, c, ctx, c_ctx, w_mod, b_mod, norm1_g, w_in, b_in, mlstm_g, sgu_ln_g, sgu_ln_b, sgu_w,
    sgu_b, conv_w, conv_b, conv_ln_g, conv_ln_b, w_out, norm2_g, w_gu, w_down, final_g, c_2,
    ctx_2, c_ctx_2, mod_w_2, mod_b_2, norm_mix_w_2, norm_ffn_w_2, ev_w_in_2, ev_w_out_2,
    ev_qn_a_2, ev_kn_a_2, ev_qn_b_2, ev_kn_b_2, ev_sink_a_2, od_w_in_2, od_w_out_2, od_qn_2,
    od_kn_2, od_lq1_2, od_lk1_2, od_lq2_2, od_lk2_2, od_subln_2, ffn_w_in_2, ffn_w_out_2,
):
    x = first_block(
        x, c, ctx, c_ctx, w_mod, b_mod, norm1_g, w_in, b_in, mlstm_g, sgu_ln_g, sgu_ln_b, sgu_w,
        sgu_b, conv_w, conv_b, conv_ln_g, conv_ln_b, w_out, norm2_g, w_gu, w_down, final_g,
    )
    return second_block(
        x, c_2, ctx_2, c_ctx_2, mod_w_2, mod_b_2, norm_mix_w_2, norm_ffn_w_2, ev_w_in_2,
        ev_w_out_2, ev_qn_a_2, ev_kn_a_2, ev_qn_b_2, ev_kn_b_2, ev_sink_a_2, od_w_in_2,
        od_w_out_2, od_qn_2, od_kn_2, od_lq1_2, od_lk1_2, od_lq2_2, od_lk2_2, od_subln_2,
        ffn_w_in_2, ffn_w_out_2,
    )


_drawn_inputs = setup_inputs


def setup_inputs(seed=0):
    import zlib

    import numpy as np

    out = dict(_drawn_inputs(seed))
    spreads = {}
    factors = {'norm1_g': 5.265,
     'mlstm_g': 8.0,
     'sgu_ln_g': 8.0,
     'sgu_ln_b': 8.0,
     'sgu_b': 8.0,
     'conv_b': 8.0,
     'conv_ln_g': 8.0,
     'conv_ln_b': 8.0,
     'norm2_g': 6.511,
     'final_g': 2.76,
     'norm_mix_w_2': 8.0,
     'norm_ffn_w_2': 6.717,
     'ev_qn_a_2': 8.0,
     'ev_kn_a_2': 8.0,
     'ev_qn_b_2': 8.0,
     'ev_kn_b_2': 8.0,
     'ev_sink_a_2': 8.0,
     'od_qn_2': 8.0,
     'od_kn_2': 8.0,
     'od_lq1_2': 64.0,
     'od_lk1_2': 64.0,
     'od_lq2_2': 4.819,
     'od_lk2_2': 53.261,
     'od_subln_2': 64.0}
    for name, (base, spread) in spreads.items():
        noise = np.random.default_rng([zlib.crc32(name.encode()), seed]).standard_normal(out[name].shape)
        drawn = base * np.exp(spread * noise) if base else spread * noise
        out[name] = __import__('jax').numpy.asarray(drawn.astype(out[name].dtype))
    for name, factor in factors.items():
        out[name] = (out[name] * factor).astype(out[name].dtype)
    return out
```

```python
import math
from contextlib import contextmanager

import numpy as np

import concourse.bass as bass
from concourse import mybir
from concourse.alu_op_type import AluOpType as ALU

F32 = mybir.dt.float32
ACT = mybir.ActivationFunctionType
AX = mybir.AxisListType
ENG = mybir.EngineType

P = 128
D = 1024
KD = D // P
SEQ = 256
TOK = 2 * SEQ
TC = TOK // P
X, C = slice(0, SEQ), slice(SEQ, TOK)
EPS = 1e-6
GRID_W = 64
HEADS, HD = 4, 128
CONV_K, HALO = 31, 15
FFN = 2816
KF = FFN // P
SGU_COL = 4 * 512 + 16
CONV_COL = SGU_COL + 512
HEAD_DIM = 64
SCALE = HEAD_DIM ** -0.5
NEG = -1e30
LAM_INIT = 0.8 - 0.6 * math.exp(-0.3)
SLOT = 11 * 256
HUGE = 3.0e38

Q_T, K_T, V_T, O_T, U_T, SV_T, CA_T, CG_T = 0, 4, 8, 12, 16, 18, 20, 22


def dyn(start, size):
    return slice(start, start + size) if isinstance(start, int) else bass.DynSlice(start, size)


class Mark:

    def __init__(self, sem, n, turn=None):
        self.sem, self.n, self.turn = sem, n, turn

    @property
    def value(self):
        return self.n if self.turn is None else self.n + self.turn[0] * self.turn[1]


class Line:

    def __init__(self, nc, eng, name):
        self.eng, self.sem, self.n, self.turn = eng, nc.alloc_semaphore(name), 0, None
        self.seen, self.seen_turn = {}, {}

    def after(self, *marks):
        for m in marks:
            if m is None:
                continue
            seen = self.seen if m.turn is None else self.seen_turn
            if seen.get(id(m.sem), -10 ** 9) >= m.n:
                continue
            if m.turn is None and self.turn is None or m.turn is not None:
                seen[id(m.sem)] = m.n
            self.eng.wait_ge(m.sem, m.value)
        return self.eng

    def step(self, instruction):
        instruction.then_inc(self.sem, 1)
        self.n += 1
        return self.here()

    def at(self, n):
        return Mark(self.sem, n, self.turn)

    def here(self):
        return Mark(self.sem, self.n, self.turn)


def program(nc, A, out):
    T = Line(nc, nc.tensor, "tensor_steps")
    V = Line(nc, nc.vector, "vector_steps")
    S = Line(nc, nc.scalar, "scalar_steps")
    G = Line(nc, nc.gpsimd, "pool_steps")
    Y = Line(nc, nc.sync, "sync_steps")
    lines = (T, V, S, G)

    def meet(*who):
        marks = [l.here() for l in lines]
        for l in who or lines:
            l.after(*marks)

    @contextmanager
    def turns_of(count, t=0, v=0, s=0, g=0):
        steps = {T: t, V: v, S: s, G: g}
        if count == 1:
            yield 0
            return
        kinds = {T: ENG.PE, V: ENG.DVE, S: ENG.Activation, G: ENG.Pool}
        used = [l for l in lines if steps[l]]
        begun = {l: l.n for l in used}
        with nc.Fori(0, count, engines=bass.OrderedEngineSet([kinds[l] for l in used])) as i:
            for l in used:
                l.turn, l.seen_turn = (i, steps[l]), {}
            yield i
        for l in used:
            assert l.n == begun[l] + steps[l], (l.n - begun[l], steps[l])
            l.n, l.turn, l.seen_turn = begun[l] + count * steps[l], None, {}

    def vtt(o, a, b, op, *after, L=V):
        return L.step(L.after(*after).tensor_tensor(o, a, b, op))

    def vts(o, a, s1, s2, op0, op1, *after, L=V):
        e = L.after(*after)
        if op1 is None:
            return L.step(e.tensor_scalar(o, a, s1, None, op0))
        return L.step(e.tensor_scalar(o, a, s1, s2, op0, op1))

    def vstt(o, a, s, b, op0, op1, *after):
        return V.step(V.after(*after).scalar_tensor_tensor(out=o, in0=a, scalar=s, in1=b, op0=op0, op1=op1))

    def vcopy(o, a, *after, L=V):
        return L.step(L.after(*after).tensor_copy(o, a))

    def act(o, a, f, *after, **k):
        return S.step(S.after(*after).activation(o, a, f, **k))

    def mm(o, w, r, start, stop, *after, done=False, shared=False):
        i = T.after(*after).matmul(o, w, r, start=start, stop=stop, skip_group_check=shared)
        return T.step(i) if done else None

    def turn(o, a, *after, done=False):
        i = T.after(*after).transpose(o, a, ident[0:a.shape[0], 0:a.shape[0]])
        return T.step(i) if done else None

    def sb(name, *shape):
        return nc.alloc_sbuf_tensor(name, list(shape), F32)

    ident = sb("ident", P, P)
    ones = sb("ones", P, P)
    mean_d = sb("mean_over_d", P, P)
    mean_c = sb("mean_over_256", P, P)
    halves = sb("mean_over_head_halves", P, P)
    swap = sb("rope_swap", P, P)
    cos = sb("cos", P, SEQ)
    sin = sb("sin", P, SEQ)
    row_of = sb("row_selectors", 64, 8, P)
    last_of = sb("last_token_selectors", P, 2, P)
    blocked = sb("blocked", P, 2, P)
    window = sb("window", P, 2, P)
    eps = sb("eps", P, 1)
    zrow = sb("zeros_row", 64, P)
    orow = sb("ones_row", 64, P)
    xT = sb("xT", P, KD, TOK)
    hT = sb("hT", P, KD, TOK)
    yT = hT
    big = sb("big", P, 24, TOK)
    ring_mem = sb("weight_slots", P, 4, SLOT)
    cols = sb("parameter_columns", P, 7, P)
    mods = sb("modulation", P, 4, 2, 48)
    coef = sb("norm_gains", P, 2, 2, KD)
    cvec = sb("condition_vectors", P, 2, KD, 2)
    sgu_wT = sb("sgu_wT", P, 2, 4, P)
    gate_raw = sb("gate_weights_raw", P, 2, KD, 16)
    evac_scale = sb("projection_scales", P, 16)
    sgu_bb = sb("sgu_bias_rows", P, 2, 2, P)
    sinks = sb("sinks", P, 8)
    nsinks = sb("minus_sinks", P, 8)
    lams = sb("lambda", P, 8)
    lamv = sb("lambda_vectors", P, 5, HEAD_DIM)
    rs = sb("rstd", P, TOK)
    gate_w = sb("gate_weights", P, KD, P)
    SCR = 13056
    scr = sb("scratch", P, SCR)

    bank = [nc.alloc_psum_tensor(f"bank{b}", [P, 512], F32) for b in range(8)]

    class Scratch:

        def __init__(self, at=0):
            self.at = at

        def __call__(self, parts, *dims):
            n = int(np.prod(dims))
            a = scr[0:parts, self.at:self.at + n]
            self.at += n
            assert self.at <= SCR, self.at
            if len(dims) > 1:
                names = "abcd"[:len(dims)]
                a = a.rearrange(f"p ({' '.join(names)}) -> p {' '.join(names)}",
                                **{x: d for x, d in zip(names, dims)})
            return a

    loads = nc.alloc_semaphore("parameter_loads")
    loads_n = [0]

    def load(dst, src):
        nc.scalar.dma_start(dst, src).then_inc(loads, 16)
        loads_n[0] += 16
        return Mark(loads, loads_n[0])

    sc = Scratch()
    rows = sc(P, 7, P)
    sgu_rows = sc(P, 2, 4, P)
    tok_in = big[:, 0:8, :].rearrange("p (c a) n -> p c (a n)", a=2)

    rows_clear = G.step(nc.gpsimd.memset(scr[:, 0:7 * P], 0.0))
    V.step(nc.vector.memset(ones[:, :], 1.0))
    V.step(nc.vector.memset(mean_d[:, :], 1.0 / D))
    V.step(nc.vector.memset(mean_c[:, :], 1.0 / 256))
    V.step(nc.vector.memset(eps[:, :], EPS))
    V.step(nc.vector.memset(zrow[:, :], 0.0))
    V.step(nc.vector.memset(orow[:, :], 1.0))
    V.step(nc.vector.memset(gate_w[:, :, :], 0.0))
    V.step(nc.vector.memset(evac_scale[:, :], 1.0))
    V.step(V.after(V.here()).memset(evac_scale[:, K_T:K_T + 4], HD ** -0.5))

    load(ident[:, :], A["k_ident"])
    S.after(rows_clear)

    def load_rows(table, at, src):
        n, w = src.shape
        load(rows[at:at + n, table, 0:w], src)

    def vec(a):
        return a.rearrange("(r p) -> r p", p=P)

    G_TAB, CW_TAB, L_TAB = 0, (1, 2), (3, 4, 5, 6)
    for at, name in ((0, "c"), (8, "c_ctx"), (16, "c_2"), (24, "c_ctx_2"), (32, "final_g")):
        a = A[name]
        load_rows(G_TAB, at, vec(a if len(a.shape) == 1 else a[0]))
    B_MOD, N1, N2 = 0, 48, 56
    B_QKVO, B_SC, M_G, SL_G, SL_B, C_B, CL_G, CL_B, B_GATE = 64, 80, 88, 92, 94, 96, 98, 100, 102
    QN_A, KN_A, QN_B, KN_B, SUB = 64, 65, 66, 67, 68
    for l in range(2):
        t = L_TAB[l]
        b_in = A["b_in"][l]
        load_rows(t, B_MOD, vec(A["b_mod"][l]))
        load_rows(t, N1, vec(A["norm1_g"][l]))
        load_rows(t, N2, vec(A["norm2_g"][l]))
        load_rows(t, B_QKVO, vec(b_in[0:2048]))
        load_rows(t, B_SC, vec(b_in[SGU_COL:SGU_COL + 1024]))
        for at, name in ((M_G, "mlstm_g"), (SL_G, "sgu_ln_g"), (SL_B, "sgu_ln_b"), (C_B, "conv_b"),
                         (CL_G, "conv_ln_g"), (CL_B, "conv_ln_b")):
            load_rows(t, at, vec(A[name][l]))
        for kind, to in enumerate((0, 64, 32, 96)):
            load(rows[B_GATE:B_GATE + 1, t, to:to + 4],
                 b_in[2048 + 4 * kind:2052 + 4 * kind].rearrange("(r p) -> r p", r=1))
        load(rows[0:2 * CONV_K, CW_TAB[l], :], A["conv_w"][l].rearrange("k (j p) -> (k j) p", p=P))
        load(sgu_rows[:, l, :, :], A["sgu_w"][l].rearrange("g p q -> p g q"))
        load(gate_raw[:, l, :, :], A["w_in"][l][:, 2048:2064].rearrange("(k p) c -> p k c", p=P))
        for j in range(2):
            for half in range(2):
                load(sgu_bb[64 * half:64 * half + 64, l, j, :],
                     A["sgu_b"][l][2 * j + half].partition_broadcast(64))
        t = L_TAB[2 + l]
        load_rows(t, B_MOD, vec(A["mod_b_2"][l]))
        load_rows(t, N1, vec(A["norm_mix_w_2"][l]))
        load_rows(t, N2, vec(A["norm_ffn_w_2"][l]))
    for t, at, name in ((L_TAB[2], QN_A, "ev_qn_a_2"), (L_TAB[2], KN_A, "ev_kn_a_2"), (L_TAB[2], QN_B, "ev_qn_b_2"),
                        (L_TAB[2], KN_B, "ev_kn_b_2"), (L_TAB[3], QN_A, "od_qn_2"), (L_TAB[3], KN_A, "od_kn_2")):
        for half in range(2):
            load(rows[at:at + 1, t, 64 * half:64 * half + 64], A[name])
    load(rows[SUB:SUB + 1, L_TAB[3], :], A["od_subln_2"])
    load(sinks[:, :], A["ev_sink_a_2"][0].partition_broadcast(P))
    for n, name in enumerate(("od_lq1_2", "od_lk1_2", "od_lq2_2", "od_lk2_2")):
        load(lamv[:, n, :], A[name][0].partition_broadcast(P))
    for dst, name in ((halves[:, :], "k_halves"), (swap[:, :], "k_swap"), (cos[:, :], "k_cos"), (sin[:, :], "k_sin"),
                      (row_of[:, :, :], "k_row_of"), (last_of[:, :, :], "k_last_of"), (blocked[:, :, :], "k_blocked"),
                      (window[:, :, :], "k_window")):
        load(dst, A[name])
    for c in range(2):
        load(tok_in[:, c, :], A["x"][0][c * P:(c + 1) * P, :])
        loaded = load(tok_in[:, 2 + c, :], A["ctx"][0][c * P:(c + 1) * P, :])
    for l in lines:
        l.after(loaded)

    meet()
    done = [turn(bank[t][:, 0:P], rows[:, t, :], done=True) for t in range(7)]
    for t in range(7):
        vcopy(cols[:, t, :], bank[t][:, 0:P], done[t])

    def tokens_in(chunks, *free):
        lo, n = chunks[0] * P, len(chunks) * P
        for k in range(KD):
            b = bank[k % 4]
            for j, c in enumerate(chunks):
                m = turn(b[:, j * P:(j + 1) * P], tok_in[:, c, k * P:(k + 1) * P],
                         *free, *(moved[k % 4:k % 4 + 1] if k >= 4 else ()), done=j == len(chunks) - 1)
            got = act(xT[:, k, lo:lo + n], b[:, 0:n], ACT.Copy, m)
            moved[k % 4] = got

    moved = [V.here()] * 4
    tokens_in(range(TC), V.here())
    meet()
    for l in range(2):
        for g in range(4):
            m = turn(bank[4 + l][:, g * P:(g + 1) * P], sgu_rows[:, l, g, :], done=g == 3)
        vcopy(sgu_wT[:, l, :, :], bank[4 + l][:, :].rearrange("p (g q) -> p g q", g=4), m)
        k_bias = cols[:, L_TAB[l], B_QKVO + 4:B_QKVO + 8]
        vts(k_bias, k_bias, HD ** -0.5, None, ALU.mult, None)

    def column(table, at, n=1):
        return cols[:, table, at:at + n]

    for blk in range(2):
        for v in range(2):
            act(cvec[:, blk, :, v], column(G_TAB, 16 * blk + 8 * v, KD), ACT.Silu)
    vts(nsinks[:, :], sinks[:, :], -1.0, None, ALU.mult, None)
    for n in range(2):
        m = vtt(lamv[:, 4, :], lamv[:, 2 * n, :], lamv[:, 2 * n + 1, :], ALU.mult, V.here())
        m = V.step(V.after(m).tensor_reduce(lams[:, n:n + 1], lamv[:, 4, :], AX.X, ALU.add))
        act(lams[:, 2 + n:3 + n], lams[:, n:n + 1], ACT.Exp, m)
    m = vtt(lams[:, 4:5], lams[:, 3:4], lams[:, 2:3], ALU.subtract, S.here())
    vts(lams[:, 5:6], lams[:, 4:5], LAM_INIT, None, ALU.subtract, None, m)
    minus_lam = lams[:, 5:6]

    class Ring:
        def __init__(self, name, slots):
            self.slots, self.next = slots, 0
            self.sems = [nc.alloc_semaphore(f"{name}{s}") for s in range(len(slots))]
            self.filled = [0] * len(slots)
            self.read = [[] for _ in slots]

    main = Ring("weights", [ring_mem[:, s, :] for s in range(4)])
    side = Ring("side_weights", [scr[:, 2048 + s * 2048:2048 + (s + 1) * 2048] for s in range(4)])

    class Feed:

        def __init__(self, turns):
            self.turns, self.items = turns, []

        def add(self, ring, source):
            s = ring.next % len(ring.slots)
            ring.next += 1
            assert all((r, x) != (ring, s) for r, x, *_ in self.items)
            item = [ring, s, source, ring.filled[s], None]
            self.items.append(item)
            Y.after(*ring.read[s])
            self.fetch(item, 0)
            return item

        def fetch(self, item, i):
            ring, s, source = item[:3]
            src = source(i)
            dst = ring.slots[s][:, 0:src.shape[1] * src.shape[2]].rearrange("p (k c) -> p k c", k=src.shape[1])
            nc.sync.dma_start(dst, src).then_inc(ring.sems[s], 16)

        def wait(self, item, i):
            nc.tensor.wait_ge(item[0].sems[item[1]], item[3] + 16 + 16 * i)
            ring, s, source = item[:3]
            k, c = source(0).shape[1:3]
            return ring.slots[s][:, 0:k * c].rearrange("p (k c) -> p k c", k=k)

        def used(self, item, mark):
            item[4] = mark

        def close(self):
            if self.turns > 1:
                with nc.sync.Fori(0, self.turns - 1) as i:
                    for item in self.items:
                        m = item[4]
                        nc.sync.wait_ge(m.sem, m.n + i * m.turn[1])
                        self.fetch(item, i + 1)
            for ring, s, _, filled, m in self.items:
                ring.filled[s] = filled + 16 * self.turns
                per = m.turn[1] if m.turn else 0
                ring.read[s] = [Mark(m.sem, m.n + (self.turns - 1) * per)]

    def block_of(w, r0, nk, col, n=256):
        return w[r0:r0 + nk * P, dyn(col, n)].rearrange("(k p) c -> p k c", p=P)

    class Banks:

        def __init__(self, ids):
            self.ids, self.n, self.free = ids, 0, {b: [] for b in ids}

        def take(self):
            b = self.ids[self.n % len(self.ids)]
            self.n += 1
            return b

    def mod_slot(w, blk, l4, item, feed, i, first_tile, b, free):
        ws = feed.wait(item, i)
        for t in range(2):
            for k in range(KD):
                m = mm(bank[b][:, 2 * t:2 * t + 2], ws[:, k, t * P:(t + 1) * P], cvec[:, blk, k, :],
                       k == 0, k == KD - 1, *(free if t == k == 0 else ()), done=(t == 1 and k == KD - 1))
        feed.used(item, m)
        for v in range(2):
            r = vtt(mods[:, l4, v, dyn(first_tile, 2)],
                    bank[b][:, 0:4].rearrange("p (t v) -> p t v", v=2)[:, :, v],
                    cols[:, L_TAB[l4], dyn(B_MOD + first_tile, 2)], ALU.add, m)
        return r

    def mod_stage(w, blk, l4):
        meet()
        with_turns = 6
        feed = Feed(with_turns)
        items = [feed.add(main, lambda i, j=j: block_of(w, 0, KD, i * 1024 + 256 * j)) for j in range(4)]
        with turns_of(with_turns, t=4, v=8) as i:
            v0 = V.n
            for j in range(4):
                mod_slot(w, blk, l4, items[j], feed, i, 8 * i + 2 * j, 4 + j, [V.at(v0 + 2 * (j - 3))])
        feed.close()
        gains(l4)

    def gains(l4):
        meet(V)
        for n, (at, s) in enumerate(((N1, 8), (N2, 32))):
            for v in range(2):
                vstt(coef[:, n, v, :], mods[:, l4, v, s:s + KD], 1.0, column(L_TAB[l4], at, KD), ALU.add, ALU.mult)

    def squares_mean(n, sc):
        sq = sc(P, KD, TOK)
        for k in range(KD):
            m = (act(sq[:, k, 0:n], xT[:, k, 0:n], ACT.Square) if k % 2 else
                 vtt(sq[:, k, 0:n], xT[:, k, 0:n], xT[:, k, 0:n], ALU.mult))
            t = mm(bank[0][:, 0:n], mean_d[:, :], sq[:, k, 0:n], k == 0, k == KD - 1, m, done=k == KD - 1)
        return rsqrt(rs[:, 0:n], bank[0][:, 0:n], t)

    def rsqrt(o, a, *after, scale=1.0):
        m = act(o, a, ACT.Ln, *after, bias=eps[0:o.shape[0], :], scale=scale)
        return act(o, o, ACT.Exp, m, scale=-0.5)

    def normed(which, l4, n):
        meet()
        r = squares_mean(n, Scratch())
        for k in range(KD):
            for v in range(n // SEQ):
                t = slice(v * SEQ, (v + 1) * SEQ)
                m = vstt(hT[:, k, t], xT[:, k, t], coef[:, which, v, k:k + 1], rs[:, t], ALU.mult, ALU.mult, r)
                act(hT[:, k, t], hT[:, k, t], ACT.Identity, m, bias=mods[:, l4, v, 24 * which + k:24 * which + k + 1])
        T.after(S.here())

    def project(w, turns, slots, n_of, evacuate, first=0):
        feed = Feed(turns)
        items = [feed.add(main, lambda i, f=f: block_of(w, 0, KD, f(i)[0])) for f in slots]
        with turns_of(turns, t=2 * len(slots), s=2 * len(slots)) as i:
            s0 = S.n
            for j, f in enumerate(slots):
                ws = feed.wait(items[j], i)
                for t in range(2):
                    e = 2 * j + t
                    free = S.at(s0 + e - 3)
                    b, n = bank[(first + e) % 4], n_of(j)
                    for k in range(KD):
                        m = mm(b[:, 0:n], ws[:, k, t * P:(t + 1) * P], hT[:, k, 0:n], k == 0, k == KD - 1,
                               free if k == 0 else None, done=k == KD - 1)
                    evacuate(f(i)[1] + t, b[:, 0:n], n, m)
                feed.used(items[j], m)
        feed.close()

    def residual(w, turns, nk, src, l4, gate, n):
        halves_ = 2 if nk > 11 else 1
        per = nk // halves_
        pairs = 4 // halves_
        feed = Feed(turns)
        items = [feed.add(main, lambda i, p=p, h=h: block_of(w, h * per * P, per, 256 * (pairs * i + p)))
                 for p in range(pairs) for h in range(halves_)]
        streams = n // SEQ
        with turns_of(turns, t=2 * pairs, v=2 * pairs * streams) as i:
            v0 = V.n
            for p in range(pairs):
                for t in range(2):
                    e = 2 * p + t
                    free = V.at(v0 + streams * (e - 3))
                    for h in range(halves_):
                        ws = feed.wait(items[p * halves_ + h], i) if t == 0 else \
                            main.slots[items[p * halves_ + h][1]][:, 0:per * 256].rearrange("p (k c) -> p k c", k=per)
                        for k in range(per):
                            kk = h * per + k
                            m = mm(bank[e % 4][:, 0:n], ws[:, k, t * P:(t + 1) * P], src[:, kk, 0:n], kk == 0,
                                   kk == nk - 1, free if kk == 0 else None, done=kk == nk - 1)
                    if t == 1:
                        for h in range(halves_):
                            feed.used(items[p * halves_ + h], m)
                    f = 2 * pairs * i + e
                    for v in range(streams):
                        tk = slice(v * SEQ, (v + 1) * SEQ)
                        o = xT[:, dyn(f, 1), tk].rearrange("p a n -> p (a n)")
                        vstt(o, bank[e % 4][:, tk], mods[:, l4, v, dyn(gate + f, 1)], o, ALU.mult, ALU.add, m)
        feed.close()

    def feed_forward(w_gu, w_down, l4, n, nxt):
        normed(1, l4, n)
        meet()
        for s in range(4):
            side.read[s] = [l.here() for l in lines]
        silu = scr[:, 0:2 * TOK].rearrange("p (b n) -> p b n", b=2)
        if nxt:
            w_mod, blk, nl4 = nxt

        def some(turns, pairs, p0, mod_slots, m0):
            feed = Feed(turns)
            items = []
            for p in range(pairs):
                for part in range(2):
                    items.append(feed.add(main, lambda i, p=p, part=part: block_of(
                        w_gu, 0, KD, 256 * (pairs * i + p + p0) + part * FFN)))
            if nxt:
                mitems = [feed.add(side, lambda i, j=j: block_of(w_mod, 0, KD, 256 * (mod_slots * i + j + m0)))
                          for j in range(mod_slots)]
            tiles = 2 * pairs
            v_per = tiles + (2 * mod_slots if nxt else 0)
            with turns_of(turns, t=2 * tiles + (mod_slots if nxt else 0), s=tiles, v=v_per) as i:
                s0, v0 = S.n, V.n
                m_per_tile = mod_slots // tiles if nxt else 0
                v_of = lambda e: V.at(v0 + e * (1 + 2 * m_per_tile) + 1)
                mod_of = lambda j: V.at(v0 + (j // m_per_tile) * (1 + 2 * m_per_tile) + 1 + 2 * (j % m_per_tile) + 2)
                for p in range(pairs):
                    gw = feed.wait(items[2 * p], i)
                    for t in range(2):
                        e = 2 * p + t
                        bg, bu = bank[2 * (e % 2)], bank[2 * (e % 2) + 1]
                        s_free, v_free = S.at(s0 + e - 1), v_of(e - 2)
                        for k in range(KD):
                            mg = mm(bg[:, 0:n], gw[:, k, t * P:(t + 1) * P], hT[:, k, 0:n], k == 0, k == KD - 1,
                                    s_free if k == 0 else None, done=k == KD - 1)
                        if t == 0:
                            uw = feed.wait(items[2 * p + 1], i)
                        for k in range(KD):
                            mu = mm(bu[:, 0:n], uw[:, k, t * P:(t + 1) * P], hT[:, k, 0:n], k == 0, k == KD - 1,
                                    v_free if k == 0 else None, done=k == KD - 1)
                        if t == 1:
                            feed.used(items[2 * p], mg)
                            feed.used(items[2 * p + 1], mu)
                        silu_done = act(silu[:, e % 2, 0:n], bg[:, 0:n], ACT.Silu, mg, v_free)
                        f = 2 * (pairs * i + p + p0) + t
                        vtt(big[:, dyn(f, 1), 0:n].rearrange("p a n -> p (a n)"), silu[:, e % 2, 0:n],
                            bu[:, 0:n], ALU.mult, silu_done, mu)
                        for q in range(m_per_tile):
                            j = m_per_tile * e + q
                            mod_slot(w_mod, blk, nl4, mitems[j], feed, i, 2 * (mod_slots * i + j + m0), 6 + j % 2,
                                     [mod_of(j - 2)])
            feed.items.sort(key=lambda it: it[4].n)
            feed.close()

        some(5, 2, 0, 4, 0)
        meet()
        some(1, 1, 10, 4, 20)
        meet()
        residual(w_down, 2, KF, big, l4, 40, n)
        meet()
        if nxt:
            gains(nl4)

    def layer_norm(src, gain, bias, n, sc, b, func, out, ready):
        d, sq, r2 = sc(P, 2, TOK), sc(P, 2, TOK), sc(P, TOK)
        for j in range(2):
            m = mm(bank[b][:, 0:n], mean_c[:, :], src[:, j, 0:n], j == 0, j == 1, *ready, done=j == 1)
        for j in range(2):
            c = vtt(d[:, j, 0:n], src[:, j, 0:n], bank[b][:, 0:n], ALU.subtract, m)
            q = act(sq[:, j, 0:n], d[:, j, 0:n], ACT.Square, c)
            t = mm(bank[b + 1][:, 0:n], mean_c[:, :], sq[:, j, 0:n], j == 0, j == 1, q, done=j == 1)
        r = rsqrt(r2[:, 0:n], bank[b + 1][:, 0:n], t)
        for j in range(2):
            m = vstt(d[:, j, 0:n], d[:, j, 0:n], gain[:, j:j + 1], r2[:, 0:n], ALU.mult, ALU.mult, r)
            done = act(out(j), d[:, j, 0:n], func, m, bias=bias[:, j:j + 1])
        return done

    def gates_rows(tab, sc):
        i_, lf, a, b_, M_ = (sc(64, TOK) for _ in range(5))
        r1, r2 = sc(P, TOK), sc(P, TOK)
        mp, nml = sc(64, 5), sc(64, 4)
        gate = bank[4]
        bias = cols[:, tab, B_GATE:B_GATE + 1]
        act(i_, gate[0:64, :], ACT.Identity, bias=bias[0:64, :])
        f = act(lf, gate[64:P, :], ACT.Identity, bias=bias[64:P, :])
        m = act(a, lf, ACT.Abs, f)
        m = act(a, a, ACT.Exp, m, scale=-1.0)
        m = act(a, a, ACT.Ln, m, bias=orow[:, 0:1])
        m = vstt(lf, lf, 0.0, a, ALU.min, ALU.subtract, m)
        z = V.step(V.eng.memset(mp[:, 0:1], 0.0))

        def span(t, c, d):
            lo, hi = c * P, (c + 1) * P
            part = t[32 * d:32 * d + 32]
            return part[:, lo:hi] if d == 0 else part[:, lo:hi][:, ::-1]

        for c in range(TC):
            for d in range(2):
                s = V.step(V.after(m).tensor_tensor_scan(span(b_, c, d), orow[32 * d:32 * d + 32, :], span(lf, c, d), 0.0,
                                                         ALU.mult, ALU.add))
        g = vtt(r1[0:64, :], i_, b_, ALU.subtract, s)
        m = z
        for s in range(4):
            for d in range(2):
                c = STEPS[d][s]
                p_ = slice(32 * d, 32 * d + 32)
                q = V.step(V.after(g, m).tensor_tensor_scan(span(M_, c, d), zrow[p_, :], span(r1, c, d), mp[p_, s:s + 1],
                                                            ALU.add, ALU.max))
                end = (c + 1) * P - 1 if d == 0 else c * P
                vts(nml[p_, s:s + 1], M_[p_, end:end + 1], -1.0, None, ALU.mult, None, q)
                e = vtt(mp[p_, s + 1:s + 2], M_[p_, end:end + 1], b_[p_, end:end + 1], ALU.add, q)
            m = e
        for s in range(4):
            for d in range(2):
                c = STEPS[d][s]
                p_, t = slice(32 * d, 32 * d + 32), slice(c * P, (c + 1) * P)
                q_ = slice(64 + 32 * d, 96 + 32 * d)
                act(r1[q_, t], M_[p_, t], ACT.Exp, m, scale=-1.0, bias=mp[p_, s:s + 1])
                act(r2[q_, t], r1[p_, t], ACT.Exp, scale=1.0, bias=nml[p_, s:s + 1])
        bm = vtt(a, b_, M_, ALU.add)
        act(r2[0:64, :], a, ACT.Exp, bm, scale=-1.0)
        T.after(S.here(), V.here())
        c1, c2 = sc(P, TC, P), sc(P, TC, P)
        for r, b, o in ((r1, 5, c1), (r2, 6, c2)):
            for c in range(TC):
                t = turn(bank[b][:, c * P:(c + 1) * P], r[:, c * P:(c + 1) * P], done=c == TC - 1)
            done = vcopy(o, bank[b][:, :].rearrange("p (c r) -> p c r", c=TC), t)
        decay = sc(P, 2, TC, HEADS)
        for d in range(2):
            t = mm(bank[7][:, 16 * d:16 * d + 16], last_of[:, d, :], c1[:, :, 64 + 32 * d:68 + 32 * d], True, True, done,
                   done=d == 1)
        vcopy(decay, bank[7][:, 0:32].rearrange("p (d c h) -> p d c h", d=2, c=TC), t)
        return M_, c1, c2, decay

    STEPS = ((2, 3, 0, 1), (3, 2, 1, 0))
    G_, W_, E_, KW_ = (0, 0), (0, 64), (1, 0), (1, 64)

    def mlstm_block_mixer(l):
        last = l == 1
        n = SEQ if last else TOK
        nch = n // P
        w, tab = A["w_in"][l], L_TAB[l]
        meet()
        def small_tile(tile, ps, n_, m):
            f = ACT.Gelu_apprx_tanh if tile < CA_T else ACT.Identity if tile < CG_T else ACT.Sigmoid
            return act(big[:, tile, 0:n_], ps, f, m, bias=column(tab, B_SC + tile - U_T))

        for g, to in enumerate((0, 64, 32, 96)):
            vcopy(gate_w[:, :, to:to + 4], gate_raw[:, l, :, 4 * g:4 * g + 4])
        gates_placed = V.here()
        project(w, 1, [lambda i, j=j: (SGU_COL + 256 * j, U_T + 2 * j) for j in range(4)], lambda j: n, small_tile)
        small_ready = S.here()
        for k in range(KD):
            mm(bank[4][:, :], gate_w[:, k, :], hT[:, k, :], k == 0, k == KD - 1, gates_placed, done=k == KD - 1)

        sc = Scratch()
        H = sc(P, TC, HEADS * HD)
        co = sc(P, 2, TOK)
        after_conv = sc.at
        for j in range(2):
            y_ready = vtt(big[:, CA_T + j, 0:n], big[:, CA_T + j, 0:n], big[:, CG_T + j, 0:n], ALU.mult, small_ready)
        chains = []
        tap = lambda j, k: column(CW_TAB[l], 2 * k + j)
        y = [big[:, CA_T + j, :] for j in range(2)]
        yr, cr = y[0][:, X].rearrange("p (r w) -> p r w", w=GRID_W), co[:, 0, X].rearrange("p (r w) -> p r w", w=GRID_W)
        chains.append([(cr[:, :, max(0, -s):GRID_W - max(0, s)], yr[:, :, max(0, s):GRID_W + min(0, s)], tap(0, s + HALO))
                       for s in range(-HALO, HALO + 1) if s])
        chains.append([(co[:, 1, max(0, -s) * GRID_W:SEQ - max(0, s) * GRID_W],
                        y[1][:, max(0, s) * GRID_W:SEQ + min(0, s) * GRID_W], tap(1, s + HALO))
                       for s in range(-(SEQ // GRID_W) + 1, SEQ // GRID_W) if s])
        if not last:
            for j in range(2):
                chains.append([(co[:, j, SEQ + max(0, -s):TOK - max(0, s)],
                                y[j][:, SEQ + max(0, s):TOK + min(0, s)], tap(j, s + HALO))
                               for s in range(-HALO, HALO + 1) if s])
        for j in range(2):
            first = vts(co[:, j, 0:n], y[j][:, 0:n], tap(j, HALO), column(tab, C_B + j), ALU.mult, ALU.add, y_ready)
        past = [first] * len(chains)
        for k in range(2 * HALO):
            for q, chain in enumerate(chains):
                if k < len(chain):
                    o, i_, t_ = chain[k]
                    past[q] = vstt(o, i_, t_, o, ALU.mult, ALU.add, past[q])
        conv_done = V.here()

        def qkvo_tile(tile, ps, n_, m):
            return act(big[:, dyn(tile, 1), 0:n_].rearrange("p a n -> p (a n)"), ps, ACT.Identity, m,
                       bias=cols[:, tab, dyn(B_QKVO + tile, 1)], scale=evac_scale[:, dyn(tile, 1)])

        slots = [lambda i, j=j: (i * 1536 + 256 * j, i * 12 + 2 * j) for j in range(2)] + \
                [lambda i, j=j: (512 + i * 512 + 256 * j, 4 + i * 4 + 2 * j) for j in range(2)]
        project(w, 2, slots, lambda j: n if j < 2 else TOK, qkvo_tile)
        meet()

        rows_sc = Scratch(after_conv)
        M_, c1, c2, decay = gates_rows(tab, rows_sc)
        meet()
        lsc = Scratch(rows_sc.at)
        layer_norm(co, column(tab, CL_G, 2), column(tab, CL_B, 2), n, lsc, 0, ACT.Silu,
                   lambda j: yT[:, 6 + j, 0:n], [conv_done])
        layer_norm(big[:, SV_T:SV_T + 2, :], column(tab, SL_G, 2), column(tab, SL_B, 2), n, lsc, 2, ACT.Identity,
                   lambda j: big[:, SV_T + j, 0:n], [])
        meet()
        lsc = Scratch(rows_sc.at)
        v_tm = lsc(P, TC, 256)
        tmp = lsc(P, 2, TOK)
        for j in range(2):
            for c in range(nch):
                t = turn(bank[j][:, c * P:(c + 1) * P], big[:, SV_T + j, c * P:(c + 1) * P], done=c == nch - 1)
            m = act(v_tm[:, 0:nch, j * P:(j + 1) * P], bank[j][:, 0:n].rearrange("p (c q) -> p c q", c=nch), ACT.Copy, t)
            for half in range(2):
                for c in range(nch):
                    t = mm(bank[2 + j][64 * half:64 * half + 64, c * P:(c + 1) * P],
                           v_tm[:, c, j * P + 64 * half:j * P + 64 * half + 64], sgu_wT[:, l, 2 * j + half, :], True, True, m,
                           done=half == 1 and c == nch - 1)
            m = vtt(tmp[:, j, 0:n].rearrange("p (c q) -> p c q", c=nch), bank[2 + j][:, 0:n].rearrange("p (c q) -> p c q", c=nch),
                    sgu_bb[:, l, j, :].unsqueeze(1).to_broadcast([P, nch, P]), ALU.add, t)
            vtt(yT[:, 4 + j, 0:n], tmp[:, j, 0:n], big[:, U_T + j, 0:n], ALU.mult, m)
        meet()
        W1 = HD + 1
        hsc = Scratch(rows_sc.at)
        spare = big[:, U_T:24, :]
        k_tm = spare[:, 0:4, :].rearrange("p c (h q) -> p c h q", h=HEADS)
        v_x = hsc(P, TC, HEADS, W1)
        G.step(G.eng.memset(v_x[:, :, :, HD:W1], 1.0))
        moved_ = [[], []]
        for h in range(HEADS):
            for s, (tile, o) in enumerate(((K_T, k_tm), (V_T, v_x))):
                b = 2 * (h % 2) + s
                for c in range(TC):
                    t = turn(bank[b][:, c * P:(c + 1) * P], big[:, tile + h, c * P:(c + 1) * P],
                             *(moved_[s][h - 2:h - 1] if h > 1 else ()), done=c == TC - 1)
                src = bank[b][:, :].rearrange("p (c q) -> p c q", c=TC)
                moved_[s].append(act(o[:, :, h, 0:HD], src, ACT.Copy, t) if s else vcopy(o[:, :, h, 0:HD], src, t))
        meet()
        E, sT = spare[:, 4:6, :], spare[:, 6:8, :]
        ks, Cst = hsc(P, 2, 3, HD), hsc(P, 2, 3, W1)
        hx = hsc(P, 2, TC, W1)
        den = hsc(P, 2, TC)
        hb = hsc(P, TC, HD)

        def col(kind, c, d, h):
            t, at = (c1, c2)[kind[0]], kind[1] + 32 * d + h
            return t[:, c, at:at + 1]

        free = {b: [] for b in range(8)}
        h_added = None
        past_sT, past_ks, past_C, past_hx = {}, {}, {}, {}
        for h in range(HEADS):
            for c in range(nch):
                t = slice(c * P, (c + 1) * P)
                s_done = mm(bank[0][:, t], big[:, K_T + h, t], big[:, Q_T + h, t], True, True, *free[0], done=c == nch - 1)
            free[0] = []
            for d in range(2):
                r = d
                m_done = mm(bank[1 + d][:, 0:n], row_of[:, 4 * d + h, :], M_[:, 0:n], True, True, *free[1 + d], done=True)
                for c in range(nch):
                    t = slice(c * P, (c + 1) * P)
                    e = vstt(E[:, d, t], bank[1 + d][:, t], col(G_, c, d, h), blocked[:, d, :], ALU.subtract, ALU.max,
                             m_done, past_sT.get(d))
                free[1 + d] = [e]
                for s in range(3):
                    c = STEPS[d][s]
                    kd = vts(ks[:, r, s, :], k_tm[:, c, h, :], col(KW_, c, d, h), None, ALU.mult, None, past_ks.get(r))
                e = act(E[:, d, 0:n], E[:, d, 0:n], ACT.Exp, e, scale=-1.0)
                sd = vtt(sT[:, d, 0:n], E[:, d, 0:n], bank[0][:, 0:n], ALU.mult, e, s_done, past_hx.get(d))
                past_sT[d] = sd
                free[0].append(sd)
                for s in range(3):
                    c = STEPS[d][s]
                    o_done = mm(bank[7][:, s * W1:(s + 1) * W1], ks[:, r, s, :], v_x[:, c, h, :], True, True, kd, *free[7],
                                done=s == 2)
                past_ks[r] = o_done
                for c in range(nch):
                    i_done = mm(bank[3 + c // 2][:, (c % 2) * W1:(c % 2 + 1) * W1], sT[:, d, c * P:(c + 1) * P],
                                v_x[:, c, h, :], True, True, sd, *free[3 + c // 2], done=c == nch - 1)
                cs = vcopy(Cst[:, r, 0, :], bank[7][:, 0:W1], o_done, past_C.get(r))
                for s in range(1, 3):
                    cs = vstt(Cst[:, r, s, :], Cst[:, r, s - 1, :], decay[:, d, STEPS[d][s], h:h + 1],
                              bank[7][:, s * W1:(s + 1) * W1], ALU.mult, ALU.add, cs)
                free[7] = [cs]
                for q in range(nch // 2):
                    x = act(hx[:, r, 2 * q:2 * q + 2, :], bank[3 + q][:, 0:2 * W1].rearrange("p (c q) -> p c q", c=2), ACT.Copy,
                            i_done, past_hx.get(("v", r)))
                    free[3 + q] = [x]
                inter = [(s, STEPS[d][s]) for s in range(1, 4) if STEPS[d][s] < nch]
                for s, c in inter:
                    q_done = mm(bank[5 + c // 2][:, (c % 2) * W1:(c % 2 + 1) * W1], big[:, Q_T + h, c * P:(c + 1) * P],
                                Cst[:, r, s - 1, :], True, True, cs, *free[5 + c // 2], done=s == 3)
                past_C[r] = past_hx[d] = q_done
                for s, c in inter:
                    v = vstt(hx[:, r, c, :], bank[5 + c // 2][:, (c % 2) * W1:(c % 2 + 1) * W1], col(W_, c, d, h),
                             hx[:, r, c, :], ALU.mult, ALU.add, q_done, x)
                free[5] = free[6] = [v]
                de = den[:, r, 0:nch]
                raw = hx[:, r, 0:nch, HD:W1].rearrange("p c a -> p (c a)")
                m = vts(de, raw, -1.0, None, ALU.mult, None, v, x)
                m = vtt(de, de, raw, ALU.max, m)
                m = vtt(de, de, c2[:, 0:nch, 32 * d + h:32 * d + h + 1].rearrange("p c a -> p (c a)"), ALU.max, m)
                m = V.step(V.after(m).reciprocal(de, de))
                num, rb = hx[:, r, 0:nch, 0:HD], de.unsqueeze(2).to_broadcast([P, nch, HD])
                Hh = H[:, 0:nch, h * HD:(h + 1) * HD]
                if d == 0:
                    h_added = vtt(Hh, num, rb, ALU.mult, m)
                else:
                    m = vtt(hb[:, 0:nch, :], num, rb, ALU.mult, m)
                    h_added = vtt(Hh, Hh, hb[:, 0:nch, :], ALU.add, m)
                past_hx[("v", r)] = h_added
        meet()
        psc = Scratch(after_conv)
        sq = psc(P, TC * HEADS, HD)
        ms = psc(P, TC * HEADS)
        N = nch * HEADS
        Hv = H.rearrange("p c (h q) -> p (c h) q", h=HEADS)[:, 0:N, :]
        m = vtt(sq[:, 0:N, :], Hv, Hv, ALU.mult)
        for j in range(HEADS):
            act(big[:, O_T + j, 0:n], big[:, O_T + j, 0:n], ACT.Sigmoid)
        m = V.step(V.after(m).tensor_reduce(ms[:, 0:N], sq[:, 0:N, :], AX.X, ALU.add))
        m = rsqrt(ms[:, 0:N], ms[:, 0:N], m, scale=1.0 / HD)
        m = vtt(Hv, Hv, ms[:, 0:N].unsqueeze(2).to_broadcast([P, N, HD]), ALU.mult, m)
        for j in range(HEADS):
            for c in range(nch):
                t = turn(bank[j][:, c * P:(c + 1) * P], H[:, c, j * HD:(j + 1) * HD], m, done=c == nch - 1)
            vstt(yT[:, j, 0:n], bank[j][:, 0:n], column(tab, M_G + j), big[:, O_T + j, 0:n], ALU.mult, ALU.mult, t)

    def plain_tile(tile, ps, n_, m):
        return act(big[:, dyn(tile, 1), 0:n_].rearrange("p a n -> p (a n)"), ps, ACT.Copy, m)

    def norm_rope(tiles, sc):
        sq, r_, t1 = sc(P, 2, TOK), sc(P, 2, TOK), sc(P, 2, SEQ)
        free = {}
        for e, (tile, gain, n_) in enumerate(tiles):
            p_ = e % 2
            x = big[:, tile, 0:n_]
            xx = big[:, tile, X]
            q = act(sq[:, p_, 0:n_], x, ACT.Square, free.get(("sq", p_)))
            s = mm(bank[p_][:, 0:n_], halves[:, :], sq[:, p_, 0:n_], True, True, q, free.get(("b", p_)), done=True)
            free["sq", p_] = s
            r = rsqrt(r_[:, p_, 0:n_], bank[p_][:, 0:n_], s, *[free.get(("r", p_))])
            free["b", p_] = r
            m = vstt(x, x, gain, r_[:, p_, 0:n_], ALU.mult, ALU.mult, r)
            free["r", p_] = m
            s = mm(bank[2 + p_][:, X], swap[:, :], xx, True, True, m, free.get(("c", p_)), done=True)
            m = vtt(t1[:, p_, :], bank[2 + p_][:, X], sin[:, :], ALU.mult, s)
            free["c", p_] = m
            c_ = vtt(xx, xx, cos[:, :], ALU.mult, s)
            vtt(xx, xx, t1[:, p_, :], ALU.add, m, c_)

    def to_tokens(tile, o, b, *after):
        for c in range(TC):
            t = turn(bank[b][:, c * P:(c + 1) * P], big[:, tile, c * P:(c + 1) * P], *after, done=c == TC - 1)
        return vcopy(o, bank[b][:, :].rearrange("p (c q) -> p c q", c=TC), t)

    def attend(units, sc, o_tm, width, combine):
        nm_ = len(units[0]["maps"])
        RP, RT = 4, 3
        Pb = sc(P, RP, nm_, TOK)
        PT = sc(P, RT, TOK)
        st = sc(P, 8, nm_, 6)
        s_banks, t_banks, o_banks = ([0, 1, 2, 7], [3, 4], [5, 6])
        free = {b: [] for b in range(8)}
        p_read, pt_read, st_read = {}, {}, {}
        used = [0]

        def scores(u, e):
            k0 = u["key0"]
            nk = TOK - k0
            u["p"] = []
            for a, (q, kk) in enumerate(u["maps"]):
                b = s_banks[used[0] % 4]
                used[0] += 1
                s = mm(bank[b][:, 0:nk], q, kk[:, k0:TOK], True, u["mask"] is None, *free[b], done=u["mask"] is None,
                       shared=True)
                if u["mask"] is not None:
                    at, which = u["mask"]
                    s = mm(bank[b][:, at:at + P], ident[:, :], window[:, which, :], False, True, done=True, shared=True)
                t = st[:, e % 8, a, :]
                m = V.step(V.after(s, st_read.get(e - 8)).tensor_reduce(t[:, 0:1], bank[b][:, 0:nk], AX.X, ALU.max))
                if u["sink"] is None:
                    m = vts(t[:, 1:2], t[:, 0:1], -SCALE, None, ALU.mult, None, m)
                else:
                    m = vts(t[:, 1:2], t[:, 0:1], -SCALE, nsinks[:, u["sink"]:u["sink"] + 1], ALU.mult, ALU.min, m)
                x = act(Pb[:, e % RP, a, 0:nk], bank[b][:, 0:nk], ACT.Exp, m, p_read.get(e - RP), scale=SCALE,
                        bias=t[:, 1:2], accum_out=t[:, 2:3])
                free[b] = [x]
                if u["sink"] is not None:
                    x = act(t[:, 3:4], sinks[:, u["sink"]:u["sink"] + 1], ACT.Exp, bias=t[:, 1:2])
                u["p"].append(x)

        def turned(u, e):
            nk = TOK - u["key0"]
            x = combine(u, e, Pb, st, nk)
            b = t_banks[e % 2]
            for c in range(nk // P):
                t = turn(bank[b][:, c * P:(c + 1) * P], Pb[:, e % RP, 0, c * P:(c + 1) * P], x, *free[b], done=c == nk // P - 1)
            p_read[e] = t
            if e % 2:
                u["pt"] = act(PT[:, e % RT, 0:nk], bank[b][:, 0:nk], ACT.Copy, t, pt_read.get(e - RT))
            else:
                u["pt"] = vcopy(PT[:, e % RT, 0:nk], bank[b][:, 0:nk], t, pt_read.get(e - RT))
            free[b] = [u["pt"]]

        def product(u, e):
            nk = TOK - u["key0"]
            c0 = u["key0"] // P
            b = o_banks[e % 2]
            for c in range(nk // P):
                m = mm(bank[b][:, 0:width], PT[:, e % RT, c * P:(c + 1) * P], u["v"](c0 + c), c == 0, c == nk // P - 1,
                       u["pt"], *free[b], done=c == nk // P - 1)
            pt_read[e] = m
            r = st[:, e % 8, 0, 5:6]
            if nm_ == 1:
                free[b] = [vts(u["out"], bank[b][:, 0:width], r, None, ALU.mult, None, m, u["rcp"])]
            else:
                free[b] = [vcopy(u["out"], bank[b][:, 0:width], m)]
            st_read[e] = free[b][0]

        for e in range(len(units) + 3):
            if e < len(units):
                scores(units[e], e)
            if 2 <= e < len(units) + 2:
                turned(units[e - 2], e - 2)
            if 3 <= e:
                product(units[e - 3], e - 3)

    def one_map(u, e, Pb, st, nk):
        t = st[:, e % 8, 0, :]
        if u["sink"] is None:
            u["rcp"] = V.step(V.after(*u["p"]).reciprocal(t[:, 5:6], t[:, 2:3]))
        else:
            m = vtt(t[:, 4:5], t[:, 2:3], t[:, 3:4], ALU.add, *u["p"])
            u["rcp"] = V.step(V.after(m).reciprocal(t[:, 5:6], t[:, 4:5]))
        return u["p"][0]

    def two_maps(u, e, Pb, st, nk):
        t = st[:, e % 8, :, :]
        for a in range(2):
            m = V.step(V.after(*u["p"]).reciprocal(t[:, a, 5:6], t[:, a, 2:3]))
        m = vtt(t[:, 1, 4:5], t[:, 1, 5:6], minus_lam, ALU.mult, m)
        p0, p1 = Pb[:, e % 4, 0, 0:nk], Pb[:, e % 4, 1, 0:nk]
        n_ = vts(p0, p0, t[:, 0, 5:6], None, ALU.mult, None, m)
        return vstt(p0, p1, t[:, 1, 4:5], p0, ALU.mult, ALU.add, n_, m)

    def from_tokens(o_tm, chunks, gain):
        done = {}
        for k in range(KD):
            b = k % 4
            for j in range(chunks):
                t = turn(bank[b][:, j * P:(j + 1) * P], o_tm[:, j, k * P:(k + 1) * P], done.get(k - 4), done=j == chunks - 1)
            o, i_ = yT[:, k, 0:chunks * P], bank[b][:, 0:chunks * P]
            if gain is None:
                done[k] = act(o, i_, ACT.Copy, t) if k % 2 else vcopy(o, i_, t)
            else:
                done[k] = vts(o, i_, gain, 1.0 - LAM_INIT, ALU.mult, ALU.mult, t)

    def even_mixer():
        tab = L_TAB[2]
        meet()
        for j in range(6):
            project(A["ev_w_in_2"][0], 1, [lambda i, j=j: (256 * j, 2 * j)], lambda _: TOK, plain_tile, first=2 * j)
        meet()
        sc = Scratch()
        norm_rope([(t, column(tab, QN_A if t < 4 else KN_A if t == 4 else QN_B if t < 10 else KN_B), TOK)
                   for t in (4, 0, 1, 2, 3, 10, 6, 7, 8, 9)], sc)
        meet()
        sc = Scratch()
        kd = sc(P, 2, 2, TOK)
        v_tm = sc(P, 2, TC, P)
        o_tm = sc(P, TC, D)
        for a, (kt, vt) in enumerate(((4, 5), (10, 11))):
            for h in range(2):
                for half in range(2):
                    act(kd[64 * half:64 * half + 64, a, h, :], big[64 * h:64 * h + 64, kt, :], ACT.Copy)
            to_tokens(vt, v_tm[:, a, :, :], 6 + a)
        meet()
        units = []
        for a in range(2):
            for h in range(8):
                kv, half = h // 4, h % 2
                tile = 6 * a + h // 2
                ps = slice(64 * half, 64 * half + 64)
                for tb in range(TC):
                    units.append(dict(
                        maps=[(big[ps, tile, tb * P:(tb + 1) * P], kd[ps, a, kv, :])],
                        key0=0 if tb < 2 else SEQ,
                        mask=((1 - tb) * P, tb) if a == 0 and tb < 2 else None,
                        sink=h if a == 0 else None,
                        v=lambda c, a=a, kv=kv: v_tm[:, a, c, 64 * kv:64 * kv + 64],
                        out=o_tm[:, tb, (8 * a + h) * 64:(8 * a + h + 1) * 64]))
        attend(units, sc, o_tm, HEAD_DIM, one_map)
        meet()
        from_tokens(o_tm, TC, None)

    def odd_mixer():
        tab = L_TAB[3]
        w = A["od_w_in_2"][0]
        meet()
        project(w, 1, [lambda i, j=j: (256 * j, 2 * j) for j in range(4)], lambda _: SEQ, plain_tile)
        meet()
        project(w, 2, [lambda i, j=j: (1024 + 1024 * i + 256 * j, 8 + 8 * i + 2 * j) for j in range(4)], lambda _: TOK,
                plain_tile)
        meet()
        norm_rope([(t, column(tab, QN_A if t < 8 else KN_A), SEQ if t < 8 else TOK) for t in range(16)], Scratch())
        meet()
        sc = Scratch()
        v_tm = sc(P, 8, TC, P)
        o_tm = sc(P, 2, D)
        done = {}
        for h in range(8):
            done[h] = to_tokens(16 + h, v_tm[:, h, :, :], h % 4, done.get(h - 4))
        meet()
        units = []
        for h in range(8):
            for tb in range(2):
                units.append(dict(
                    maps=[(big[64 * a:64 * a + 64, h, tb * P:(tb + 1) * P], big[64 * a:64 * a + 64, 8 + h, :]) for a in range(2)],
                    key0=0, mask=None, sink=None, v=lambda c, h=h: v_tm[:, h, c, :], out=o_tm[:, tb, h * P:(h + 1) * P]))
        attend(units, sc, o_tm, P, two_maps)
        meet()
        sc = Scratch()
        sc.at = 8 * TC * P + 2 * D
        sq, ms, ok = sc(P, 16, P), sc(P, 16), sc(P, 16)
        ov = o_tm.rearrange("p c (h q) -> p (c h) q", q=P)
        m = vts(sq, ov, 2.0 ** -40, 2.0 ** 60, ALU.mult, ALU.min)
        m = vts(sq, sq, -2.0 ** 60, None, ALU.max, None, m)
        m = vtt(sq, sq, sq, ALU.mult, m)
        m = V.step(V.after(m).tensor_reduce(ms, sq, AX.X, ALU.add))
        m = vts(ok, ms, 3.4028235e38 * 2.0 ** -80, 2.0 ** -40, ALU.is_le, ALU.mult, m)
        m = vts(ms, ms, 1.0 / P, EPS * 2.0 ** -80, ALU.mult, ALU.add, m)
        m = vts(ms, ms, 2.0 ** 100, None, ALU.min, None, m)
        m = act(ms, ms, ACT.Sqrt, m)
        m = V.step(V.after(m).reciprocal(ms, ms))
        m = vtt(ms, ms, ok, ALU.mult, m)
        vtt(ov, ov, ms.unsqueeze(2).to_broadcast([P, 16, P]), ALU.mult, m)
        meet()
        from_tokens(o_tm, 2, column(tab, SUB))

    def finish():
        meet()
        o = hT[:, 0:4, :].rearrange("p (c a) n -> p c (a n)", a=2)
        done = {}
        for k in range(KD):
            for c in range(2):
                t = turn(bank[k % 4][:, c * P:(c + 1) * P], xT[:, k, c * P:(c + 1) * P], done.get(k - 4), done=c == 1)
            done[k] = vcopy(o[:, :, k * P:(k + 1) * P], bank[k % 4][:, X].rearrange("p (c q) -> p c q", c=2), t)
        Y.after(V.here())
        stored = nc.alloc_semaphore("stored")
        for c in range(2):
            nc.sync.dma_start(out[0][c * P:(c + 1) * P, :], o[:, c, :]).then_inc(stored, 16)
        nc.sync.wait_ge(stored, 32)


    mod_stage(A["w_mod"][0], 0, 0)
    for l in range(2):
        n = TOK if l == 0 else SEQ
        normed(0, l, TOK)
        mlstm_block_mixer(l)
        meet()
        residual(A["w_out"][l], 1, KD, yT, l, 16, n)
        nxt = (A["w_mod"][1], 0, 1) if l == 0 else (A["mod_w_2"][0], 1, 2)
        feed_forward(A["w_gu"][l], A["w_down"][l], l, n, nxt)
    meet()
    loaded = []
    for c in range(2):
        loaded.append(load(tok_in[:, 2 + c, :], A["ctx_2"][0][c * P:(c + 1) * P, :]))
    r = squares_mean(SEQ, Scratch())
    for k in range(KD):
        vstt(xT[:, k, X], xT[:, k, X], column(G_TAB, 32 + k), rs[:, X], ALU.mult, ALU.mult, r)
    moved = [V.here()] * 4
    meet()
    T.after(loaded[-1])
    tokens_in([2, 3])
    meet()
    for l in range(2):
        n = TOK if l == 0 else SEQ
        normed(0, 2 + l, TOK)
        (even_mixer if l == 0 else odd_mixer)()
        meet()
        w = A["ev_w_out_2"][0] if l == 0 else A["od_w_out_2"][0]
        residual(w, 1, KD, yT, 2 + l, 16, n)
        feed_forward(A["ffn_w_in_2"][l], A["ffn_w_out_2"][l], 2 + l, n, (A["mod_w_2"][1], 1, 3) if l == 0 else None)
    finish()


def shape_constants():
    f = np.float32
    r = np.arange(P)
    c = {"k_ident": np.eye(P, dtype=f)}
    c["k_halves"] = np.where(r[:, None] // 64 == r[None, :] // 64, 1 / 64, 0).astype(f)
    swap = np.zeros((P, P), f)
    swap[r[1::2], r[0::2]] = -1.0
    swap[r[0::2], r[1::2]] = 1.0
    c["k_swap"] = swap
    t = np.arange(SEQ)
    nf = HEAD_DIM // 4
    inv = (f(10000.0) ** (-np.arange(nf, dtype=f) / f(nf))).astype(f)
    ang = np.concatenate([(t // GRID_W).astype(f)[:, None] * inv, (t % GRID_W).astype(f)[:, None] * inv], -1)
    pair = (r % HEAD_DIM) // 2
    c["k_cos"] = np.ascontiguousarray(np.cos(ang)[:, pair].T.astype(f))
    c["k_sin"] = np.ascontiguousarray(np.sin(ang)[:, pair].T.astype(f))
    row = np.zeros((64, 8, P), f)
    for d in range(2):
        for h in range(HEADS):
            row[32 * d + h, 4 * d + h, :] = 1.0
    c["k_row_of"] = row
    last = np.zeros((P, 2, P), f)
    last[P - 1, 0, :] = 1.0
    last[0, 1, :] = 1.0
    c["k_last_of"] = last
    b = np.zeros((P, 2, P), f)
    b[:, 0, :] = np.where(r[:, None] > r[None, :], HUGE, 0)
    b[:, 1, :] = np.where(r[:, None] < r[None, :], HUGE, 0)
    c["k_blocked"] = b
    w = np.zeros((P, 2, P), f)
    w[:, 0, :] = np.where(r[None, :] <= r[:, None], 0, NEG)
    w[:, 1, :] = np.where(r[None, :] >= r[:, None], 0, NEG)
    c["k_window"] = w
    return c


_INS = ['x', 'ctx', 'c', 'c_ctx', 'w_mod', 'b_mod', 'norm1_g', 'w_in', 'b_in', 'mlstm_g', 'sgu_ln_g', 'sgu_ln_b', 'sgu_w',
        'sgu_b', 'conv_w', 'conv_b', 'conv_ln_g', 'conv_ln_b', 'w_out', 'norm2_g', 'w_gu', 'w_down', 'final_g', 'c_2',
        'ctx_2', 'c_ctx_2', 'mod_w_2', 'mod_b_2', 'norm_mix_w_2', 'norm_ffn_w_2', 'ev_w_in_2', 'ev_w_out_2', 'ev_qn_a_2',
        'ev_kn_a_2', 'ev_qn_b_2', 'ev_kn_b_2', 'ev_sink_a_2', 'od_w_in_2', 'od_w_out_2', 'od_qn_2', 'od_kn_2', 'od_lq1_2',
        'od_lk1_2', 'od_lq2_2', 'od_lk2_2', 'od_subln_2', 'ffn_w_in_2', 'ffn_w_out_2']


def kernel(**inputs):
    import concourse.bacc as bacc
    from concourse.bass_utils import run_bass_kernel_spmd

    nc = bacc.Bacc("TRN2", target_bir_lowering=False, num_devices=1)
    arrays = {n: np.ascontiguousarray(inputs[n]) for n in _INS}
    arrays.update(shape_constants())
    A = {n: nc.dram_tensor(n, a.shape, mybir.dt.from_np(a.dtype), kind="ExternalInput").ap() for n, a in arrays.items()}
    out = nc.dram_tensor("out", (1, SEQ, D), F32, kind="ExternalOutput").ap()
    program(nc, A, out)
    r = run_bass_kernel_spmd(nc, [arrays], core_ids=[0])
    return r.results[0]["out"]
```
